# Optimizing a Trainium2 kernel written in Bass

```python
import math
import jax
import jax.numpy as jnp
from jax import lax
import numpy as np

D_MODEL = 1024
BATCH = 1
SEQ = 256
DEPTH = 2

GRID_W = 64
CTX_LEN = 256
EPS = 1e-6
ROPE_BASE = 10000.0
N_MOD = 9

A_HEADS = 4
A_QK = 32
A_V = 2 * A_QK
A_QCOLS = A_HEADS * 2 * A_QK
A_COLS = 2 * A_QCOLS + A_HEADS * A_V
A_SCALE = A_QK ** -0.5
Q_BLOCK = 128

B_HEADS = 4
B_KV_HEADS = 2
B_DIM = 64
WINDOW = 128
BLOCK = 128
B_QCOLS = B_HEADS * B_DIM
B_KCOLS = B_KV_HEADS * B_DIM
B_COLS = B_QCOLS + 2 * B_KCOLS
B_SCALE = B_DIM ** -0.5

C_HEADS = 8
C_HEAD_DIM = 64
C_INNER = C_HEADS * C_HEAD_DIM
C_GROUPS = 2
C_STATE = 64
C_CONV = 5
CHUNK = 128
C_XBC = C_INNER + 2 * C_GROUPS * C_STATE
C_COLS = C_INNER + C_XBC + 2 * C_HEADS

IN_COLS = A_COLS + B_COLS + C_COLS
MIX_WIDTH = A_HEADS * A_V + B_HEADS * B_DIM + C_INNER
D_FF = 2816

kernel_name = 'hybrid_dit_diffattn_swa_ssd_macaron'

def rms_norm(x, w):
    xf = x.astype(jnp.float32)
    y = xf * lax.rsqrt(jnp.mean(xf * xf, axis=-1, keepdims=True) + EPS)
    return (y * w.astype(jnp.float32)).astype(x.dtype)

def modulate(h, shift, scale):
    return h * (1 + scale) + shift

def adaln_chunks(mod):
    m = mod.reshape(-1, 1, N_MOD, D_MODEL)
    return [m[:, :, i] for i in range(N_MOD)]

def swiglu(h, w13, w2):
    g, u = jnp.split(h @ w13, 2, axis=-1)
    return (jax.nn.silu(g) * u) @ w2

def axial_rope_tables(seq_len, dim):
    rows = seq_len // GRID_W
    row = jnp.repeat(jnp.arange(rows, dtype=jnp.float32), GRID_W)
    col = jnp.tile(jnp.arange(GRID_W, dtype=jnp.float32), rows)
    quarter = dim // 4
    inv_freq = ROPE_BASE ** (-jnp.arange(quarter, dtype=jnp.float32) / quarter)
    ar = row[:, None] * inv_freq
    ac = col[:, None] * inv_freq
    ang = jnp.concatenate([ar, ar, ac, ac], axis=-1)
    return jnp.cos(ang), jnp.sin(ang)

def axial_rope(x, cos, sin):
    d = x.shape[-1]
    half, quarter = d // 2, d // 4

    def rot(u):
        return jnp.concatenate([-u[..., quarter:], u[..., :quarter]], axis=-1)

    xr = jnp.concatenate([rot(x[..., :half]), rot(x[..., half:])], axis=-1)
    shape = (1, x.shape[1]) + (1,) * (x.ndim - 3) + (d,)
    return x * cos.reshape(shape).astype(x.dtype) + xr * sin.reshape(shape).astype(x.dtype)

def diff_heads(p, qn, kn):
    b, t = p.shape[:2]
    q = rms_norm(p[..., :A_QCOLS].reshape(b, t, A_HEADS, 2, A_QK), qn)
    k = rms_norm(p[..., A_QCOLS:2 * A_QCOLS].reshape(b, t, A_HEADS, 2, A_QK), kn)
    v = p[..., 2 * A_QCOLS:].reshape(b, t, A_HEADS, A_V)
    return q, k, v

def diff_attend(q, k, v, lam, lam_init, subln):
    s = jnp.einsum('bqhcd,bkhcd->bhcqk', q, k).astype(jnp.float32) * A_SCALE
    p = jax.nn.softmax(s, axis=-1)
    a = p[:, :, 0] - lam * p[:, :, 1]
    o = jnp.einsum('bhqk,bkhd->bqhd', a.astype(v.dtype), v)
    return rms_norm(o, subln) * (1.0 - lam_init)

def diff_attend_latent(q, k_all, v_all, lam, lam_init, subln):
    b, s = q.shape[:2]
    nb = s // Q_BLOCK
    qb = jnp.moveaxis(q.reshape((b, nb, Q_BLOCK) + q.shape[2:]), 1, 0)
    ob = lax.map(lambda qi: diff_attend(qi, k_all, v_all, lam, lam_init, subln), qb)
    return jnp.moveaxis(ob, 0, 1).reshape(b, s, A_HEADS * A_V)

def gqa_heads(p, qn, kn):
    b, t = p.shape[:2]
    q = rms_norm(p[..., :B_QCOLS].reshape(b, t, B_HEADS, B_DIM), qn)
    k = rms_norm(p[..., B_QCOLS:B_QCOLS + B_KCOLS].reshape(b, t, B_KV_HEADS, B_DIM), kn)
    v = p[..., B_QCOLS + B_KCOLS:].reshape(b, t, B_KV_HEADS, B_DIM)
    return q, k, v

def window_attend_latent(q, k, v, k_ctx, v_ctx, sink):
    b, s, hq, d = q.shape
    g = hq // B_KV_HEADS
    nb = s // BLOCK
    qb = q.reshape(b, nb, BLOCK, B_KV_HEADS, g, d)
    pad = ((0, 0), (BLOCK, BLOCK), (0, 0), (0, 0))
    kp = jnp.pad(k, pad).reshape(b, nb + 2, BLOCK, B_KV_HEADS, d)
    vp = jnp.pad(v, pad).reshape(b, nb + 2, BLOCK, B_KV_HEADS, d)
    kw = jnp.concatenate([kp[:, :-2], kp[:, 1:-1], kp[:, 2:]], axis=2)
    vw = jnp.concatenate([vp[:, :-2], vp[:, 1:-1], vp[:, 2:]], axis=2)
    s_win = jnp.einsum('bnqhgd,bnkhd->bnhgqk', qb, kw).astype(jnp.float32) * B_SCALE
    qpos = jnp.arange(nb)[:, None] * BLOCK + jnp.arange(BLOCK)[None, :]
    kpos = (jnp.arange(nb)[:, None] - 1) * BLOCK + jnp.arange(3 * BLOCK)[None, :]
    valid = ((jnp.abs(kpos[:, None, :] - qpos[:, :, None]) <= WINDOW)
             & (kpos >= 0)[:, None, :] & (kpos < s)[:, None, :])
    s_win = jnp.where(valid[None, :, None, None], s_win, -jnp.inf)
    s_ctx = jnp.einsum('bnqhgd,bkhd->bnhgqk', qb, k_ctx).astype(jnp.float32) * B_SCALE
    sink_col = jnp.broadcast_to(sink.reshape(1, 1, B_KV_HEADS, g, 1, 1).astype(jnp.float32),
                                s_win.shape[:-1] + (1,))
    p = jax.nn.softmax(jnp.concatenate([s_win, s_ctx, sink_col], axis=-1), axis=-1)
    nw, nc = 3 * BLOCK, k_ctx.shape[1]
    p_win = p[..., :nw].astype(v.dtype)
    p_ctx = p[..., nw:nw + nc].astype(v.dtype)
    o = (jnp.einsum('bnhgqk,bnkhd->bnqhgd', p_win, vw)
         + jnp.einsum('bnhgqk,bkhd->bnqhgd', p_ctx, v_ctx))
    return o.reshape(b, s, hq * d)

def sink_attend_ctx(q, k, v, sink):
    b, t, hq, d = q.shape
    g = hq // B_KV_HEADS
    qg = q.reshape(b, t, B_KV_HEADS, g, d)
    s = jnp.einsum('bqhgd,bkhd->bhgqk', qg, k).astype(jnp.float32) * B_SCALE
    sink_col = jnp.broadcast_to(sink.reshape(1, B_KV_HEADS, g, 1, 1).astype(jnp.float32), s.shape[:-1] + (1,))
    p = jax.nn.softmax(jnp.concatenate([s, sink_col], axis=-1), axis=-1)[..., :-1]
    o = jnp.einsum('bhgqk,bkhd->bqhgd', p.astype(v.dtype), v)
    return o.reshape(b, t, hq * d)

def conv_centred(u, w, bias):
    ch = u.shape[-1]
    y = lax.conv_general_dilated(u, w.reshape(C_CONV, 1, ch).astype(u.dtype), window_strides=(1,),
                                 padding=[(C_CONV // 2, C_CONV // 2)],
                                 dimension_numbers=('NWC', 'WIO', 'NWC'), feature_group_count=ch)
    return jax.nn.silu(y + bias.astype(u.dtype))

def ssm_inputs(p, conv_w, conv_b):
    b, t = p.shape[:2]
    z = p[..., :C_INNER]
    xbc = conv_centred(p[..., C_INNER:C_INNER + C_XBC], conv_w, conv_b)
    xs = xbc[..., :C_INNER].reshape(b, t, C_HEADS, C_HEAD_DIM)
    bm = xbc[..., C_INNER:C_INNER + C_GROUPS * C_STATE].reshape(b, t, C_GROUPS, C_STATE)
    cm = xbc[..., C_INNER + C_GROUPS * C_STATE:].reshape(b, t, C_GROUPS, C_STATE)
    dt_raw = p[..., C_INNER + C_XBC:].reshape(b, t, 2, C_HEADS)
    return z, xs, bm, cm, dt_raw

def segsum(a):
    t = a.shape[-1]
    rep = jnp.broadcast_to(a[..., :, None], a.shape + (t,))
    cs = jnp.cumsum(jnp.where(jnp.tril(jnp.ones((t, t), bool), -1), rep, 0.0), axis=-2)
    return jnp.where(jnp.tril(jnp.ones((t, t), bool)), cs, -jnp.inf)

def ssd_scan(x, dt, A, bm, cm, init):
    b, t, h, pdim = x.shape
    g, n = bm.shape[2], bm.shape[3]
    r = h // g
    nc = t // CHUNK
    f32 = jnp.float32
    xdt = (x.astype(f32) * dt[..., None]).reshape(b, nc, CHUNK, g, r, pdim)
    a = jnp.moveaxis((dt * A).reshape(b, nc, CHUNK, g, r), 2, -1)
    a_cs = jnp.cumsum(a, axis=-1)
    bc = bm.astype(f32).reshape(b, nc, CHUNK, g, n)
    cc = cm.astype(f32).reshape(b, nc, CHUNK, g, n)
    decay_in = jnp.exp(segsum(a))
    cb = jnp.einsum('bclgn,bcsgn->bcgls', cc, bc)
    y_diag = jnp.einsum('bcgls,bcgrls,bcsgrp->bclgrp', cb, decay_in, xdt)
    decay_to_end = jnp.exp(a_cs[..., -1:] - a_cs)
    states = jnp.einsum('bclgn,bcgrl,bclgrp->bcgrpn', bc, decay_to_end, xdt)
    states = jnp.concatenate([init[:, None].astype(f32), states], axis=1)
    chunk_a = jnp.pad(jnp.moveaxis(a_cs[..., -1], 1, -1), ((0, 0), (0, 0), (0, 0), (1, 0)))
    decay_chunk = jnp.exp(segsum(chunk_a))
    new_states = jnp.einsum('bgrzc,bcgrpn->bzgrpn', decay_chunk, states)
    y_off = jnp.einsum('bclgn,bcgrpn,bcgrl->bclgrp', cc, new_states[:, :-1], jnp.exp(a_cs))
    y = (y_diag + y_off).reshape(b, t, h, pdim).astype(x.dtype)
    return y, new_states[:, -1]

def bidir_ssd(xs_c, b_c, c_c, dtr_c, xs_l, b_l, c_l, dtr_l, dt_bias, a_log):
    bsz = xs_l.shape[0]
    init = jnp.zeros((bsz, C_GROUPS, C_HEADS // C_GROUPS, C_HEAD_DIM, C_STATE), jnp.float32)
    y_ctx, y_lat = [], []
    for direction in range(2):
        if direction == 0:
            flip = lambda u: u
        else:
            flip = lambda u: jnp.flip(u, axis=1)
        A = -jnp.exp(a_log[direction].astype(jnp.float32))
        dt_c = jax.nn.softplus(dtr_c[..., direction, :].astype(jnp.float32) + dt_bias[direction].astype(jnp.float32))
        dt_l = jax.nn.softplus(dtr_l[..., direction, :].astype(jnp.float32) + dt_bias[direction].astype(jnp.float32))
        yc, h_ctx = ssd_scan(flip(xs_c), flip(dt_c), A, flip(b_c), flip(c_c), init)
        yl, _ = ssd_scan(flip(xs_l), flip(dt_l), A, flip(b_l), flip(c_l), h_ctx)
        y_ctx.append(flip(yc))
        y_lat.append(flip(yl))
    return y_ctx[0] + y_ctx[1], y_lat[0] + y_lat[1]

def ssm_output(y, xs, z, d_skip, gnorm):
    b, t = y.shape[:2]
    y = (y + d_skip[:, None].astype(y.dtype) * xs).reshape(b, t, C_INNER) * jax.nn.silu(z)
    y = rms_norm(y.reshape(b, t, C_GROUPS, C_INNER // C_GROUPS), gnorm.reshape(C_GROUPS, C_INNER // C_GROUPS))
    return y.reshape(b, t, C_INNER)

def hybrid_mixer(h_ctx, h_lat, cos_a, sin_a, cos_b, sin_b, w_in, qn_a, kn_a, lam, lam_init, subln_a,
                 qn_b, kn_b, sink_b, conv_w, conv_b, dt_bias, a_log, d_skip, gnorm_c, with_ctx_out):
    p_ctx = h_ctx @ w_in
    p_lat = h_lat @ w_in
    o1, o2 = A_COLS, A_COLS + B_COLS
    qa_c, ka_c, va_c = diff_heads(p_ctx[..., :o1], qn_a, kn_a)
    qa_l, ka_l, va_l = diff_heads(p_lat[..., :o1], qn_a, kn_a)
    qa_l = axial_rope(qa_l, cos_a, sin_a)
    ka_l = axial_rope(ka_l, cos_a, sin_a)
    ka_all = jnp.concatenate([ka_c, ka_l], axis=1)
    va_all = jnp.concatenate([va_c, va_l], axis=1)
    oa_l = diff_attend_latent(qa_l, ka_all, va_all, lam, lam_init, subln_a)
    qb_c, kb_c, vb_c = gqa_heads(p_ctx[..., o1:o2], qn_b, kn_b)
    qb_l, kb_l, vb_l = gqa_heads(p_lat[..., o1:o2], qn_b, kn_b)
    qb_l = axial_rope(qb_l, cos_b, sin_b)
    kb_l = axial_rope(kb_l, cos_b, sin_b)
    ob_l = window_attend_latent(qb_l, kb_l, vb_l, kb_c, vb_c, sink_b)
    z_c, xs_c, b_c, c_c, dtr_c = ssm_inputs(p_ctx[..., o2:], conv_w, conv_b)
    z_l, xs_l, b_l, c_l, dtr_l = ssm_inputs(p_lat[..., o2:], conv_w, conv_b)
    y_c, y_l = bidir_ssd(xs_c, b_c, c_c, dtr_c, xs_l, b_l, c_l, dtr_l, dt_bias, a_log)
    oc_l = ssm_output(y_l, xs_l, z_l, d_skip, gnorm_c)
    out_lat = jnp.concatenate([oa_l, ob_l, oc_l], axis=-1)
    if not with_ctx_out:
        return None, out_lat
    bsz, tc = h_ctx.shape[:2]
    oa_c = diff_attend(qa_c, ka_c, va_c, lam, lam_init, subln_a).reshape(bsz, tc, A_HEADS * A_V)
    ob_c = sink_attend_ctx(qb_c, kb_c, vb_c, sink_b)
    oc_c = ssm_output(y_c, xs_c, z_c, d_skip, gnorm_c)
    out_ctx = jnp.concatenate([oa_c, ob_c, oc_c], axis=-1)
    return out_ctx, out_lat

def setup_inputs(seed: int = 0) -> dict:
    key = jax.random.key(seed)
    ks = iter(jax.random.split(key, 40))
    L = DEPTH

    def nrm(shape, scale):
        return jax.random.normal(next(ks), shape, jnp.float32) * scale

    def gain(shape):
        return 1.0 + 0.02 * jax.random.normal(next(ks), shape, jnp.float32)

    x = nrm((BATCH, SEQ, D_MODEL), 1.0)
    c = nrm((BATCH, D_MODEL), 1.0)
    ctx = nrm((BATCH, CTX_LEN, D_MODEL), 1.0)
    c_ctx = nrm((D_MODEL,), 1.0)
    w_mod = nrm((L, D_MODEL, N_MOD * D_MODEL), 0.5 * D_MODEL ** -0.5)
    b_mod = nrm((L, N_MOD * D_MODEL), 0.02)
    norm_ffn1 = gain((L, D_MODEL))
    ffn1_w13 = nrm((L, D_MODEL, 2 * D_FF), D_MODEL ** -0.5)
    ffn1_w2 = nrm((L, D_FF, D_MODEL), D_FF ** -0.5)
    norm_mix = gain((L, D_MODEL))
    w_in = nrm((L, D_MODEL, IN_COLS), D_MODEL ** -0.5)
    w_out = nrm((L, MIX_WIDTH, D_MODEL), MIX_WIDTH ** -0.5)
    qn_a = gain((L, A_QK))
    kn_a = gain((L, A_QK))
    lam_q1 = nrm((L, A_QK), 0.1)
    lam_k1 = nrm((L, A_QK), 0.1)
    lam_q2 = nrm((L, A_QK), 0.1)
    lam_k2 = nrm((L, A_QK), 0.1)
    subln_a = gain((L, A_V))
    qn_b = gain((L, B_DIM))
    kn_b = gain((L, B_DIM))
    sink_b = nrm((L, B_HEADS), 0.5)
    conv_w = nrm((L, C_CONV, C_XBC), C_CONV ** -0.5)
    conv_b = nrm((L, C_XBC), 0.01)
    dt0 = jnp.exp(jax.random.uniform(next(ks), (L, 2, C_HEADS), jnp.float32, math.log(1e-3), math.log(1e-1)))
    dt_bias = dt0 + jnp.log(-jnp.expm1(-dt0))
    a_log = jnp.log(jax.random.uniform(next(ks), (L, 2, C_HEADS), jnp.float32, 1.0, 16.0))
    d_skip = gain((L, C_HEADS))
    gnorm_c = gain((L, C_INNER))
    norm_ffn2 = gain((L, D_MODEL))
    ffn2_w13 = nrm((L, D_MODEL, 2 * D_FF), D_MODEL ** -0.5)
    ffn2_w2 = nrm((L, D_FF, D_MODEL), D_FF ** -0.5)
    return {'x': x, 'c': c, 'ctx': ctx, 'c_ctx': c_ctx, 'w_mod': w_mod, 'b_mod': b_mod,
            'norm_ffn1': norm_ffn1, 'ffn1_w13': ffn1_w13, 'ffn1_w2': ffn1_w2,
            'norm_mix': norm_mix, 'w_in': w_in, 'w_out': w_out,
            'qn_a': qn_a, 'kn_a': kn_a, 'lam_q1': lam_q1, 'lam_k1': lam_k1, 'lam_q2': lam_q2, 'lam_k2': lam_k2,
            'subln_a': subln_a, 'qn_b': qn_b, 'kn_b': kn_b, 'sink_b': sink_b,
            'conv_w': conv_w, 'conv_b': conv_b, 'dt_bias': dt_bias, 'a_log': a_log, 'd_skip': d_skip,
            'gnorm_c': gnorm_c, 'norm_ffn2': norm_ffn2, 'ffn2_w13': ffn2_w13, 'ffn2_w2': ffn2_w2}

def reference(x, c, ctx, c_ctx, w_mod, b_mod, norm_ffn1, ffn1_w13, ffn1_w2, norm_mix, w_in, w_out,
              qn_a, kn_a, lam_q1, lam_k1, lam_q2, lam_k2, subln_a, qn_b, kn_b, sink_b,
              conv_w, conv_b, dt_bias, a_log, d_skip, gnorm_c, norm_ffn2, ffn2_w13, ffn2_w2):
    s = x.shape[1]
    cos_a, sin_a = axial_rope_tables(s, A_QK)
    cos_b, sin_b = axial_rope_tables(s, B_DIM)
    sc_lat = jax.nn.silu(c)
    sc_ctx = jax.nn.silu(c_ctx)
    xl, xc = x, ctx
    for l in range(DEPTH):
        last = l == DEPTH - 1
        ml = adaln_chunks(sc_lat @ w_mod[l] + b_mod[l])
        mc = adaln_chunks(sc_ctx @ w_mod[l] + b_mod[l])
        xl = xl + 0.5 * ml[2] * swiglu(modulate(rms_norm(xl, norm_ffn1[l]), ml[0], ml[1]), ffn1_w13[l], ffn1_w2[l])
        xc = xc + 0.5 * mc[2] * swiglu(modulate(rms_norm(xc, norm_ffn1[l]), mc[0], mc[1]), ffn1_w13[l], ffn1_w2[l])
        lam_init = 0.8 - 0.6 * math.exp(-0.3 * l)
        lam = (jnp.exp(jnp.sum(lam_q1[l].astype(jnp.float32) * lam_k1[l].astype(jnp.float32)))
               - jnp.exp(jnp.sum(lam_q2[l].astype(jnp.float32) * lam_k2[l].astype(jnp.float32))) + lam_init)
        h_ctx = modulate(rms_norm(xc, norm_mix[l]), mc[3], mc[4])
        h_lat = modulate(rms_norm(xl, norm_mix[l]), ml[3], ml[4])
        mix_c, mix_l = hybrid_mixer(h_ctx, h_lat, cos_a, sin_a, cos_b, sin_b, w_in[l], qn_a[l], kn_a[l], lam,
                                    lam_init, subln_a[l], qn_b[l], kn_b[l], sink_b[l], conv_w[l], conv_b[l],
                                    dt_bias[l], a_log[l], d_skip[l], gnorm_c[l], not last)
        xl = xl + ml[5] * (mix_l @ w_out[l])
        xl = xl + 0.5 * ml[8] * swiglu(modulate(rms_norm(xl, norm_ffn2[l]), ml[6], ml[7]), ffn2_w13[l], ffn2_w2[l])
        if not last:
            xc = xc + mc[5] * (mix_c @ w_out[l])
            xc = xc + 0.5 * mc[8] * swiglu(modulate(rms_norm(xc, norm_ffn2[l]), mc[6], mc[7]), ffn2_w13[l], ffn2_w2[l])
    return xl


_drawn_inputs = setup_inputs


def setup_inputs(seed=0):
    import zlib

    import numpy as np

    out = dict(_drawn_inputs(seed))
    spreads = {}
    factors = {'norm_ffn1': 8.0,
     'norm_mix': 5.904,
     'qn_a': 8.0,
     'kn_a': 8.0,
     'lam_q1': 8.0,
     'lam_k1': 8.0,
     'lam_q2': 7.842,
     'lam_k2': 4.413,
     'subln_a': 64.0,
     'qn_b': 8.0,
     'kn_b': 8.0,
     'sink_b': 8.0,
     'conv_b': 54.456,
     'd_skip': 64.0,
     'gnorm_c': 44.355,
     'norm_ffn2': 8.0}
    for name, (base, spread) in spreads.items():
        noise = np.random.default_rng([zlib.crc32(name.encode()), seed]).standard_normal(out[name].shape)
        drawn = base * np.exp(spread * noise) if base else spread * noise
        out[name] = jnp.asarray(drawn.astype(out[name].dtype))
    for name, factor in factors.items():
        out[name] = (out[name] * factor).astype(out[name].dtype)
    return out
```

```python
import math
from contextlib import ExitStack

import numpy as np
import concourse.bass as bass
from concourse import mybir

F32 = mybir.dt.float32
F32R = mybir.dt.float32r
ALU = mybir.AluOpType
ACT = mybir.ActivationFunctionType
AX_X = mybir.AxisListType.X
LN_EXP_SET = 6

P = 128
DEPTH = 2
D_MODEL = 1024
KT = D_MODEL // P
LAT = 256
CTX = 256
T = LAT + CTX
TT = T // P
EPS = 1e-6
D_FF = 2816
PAIRS = D_FF // 256
UNIT = 2048
FFN_UNITS = 3 * PAIRS
PROJ_UNITS = 11
OUT_UNITS = 4
DT_UNIT = 5
MIX_UNITS = PROJ_UNITS + OUT_UNITS
LAYER_UNITS = 2 * FFN_UNITS + MIX_UNITS
A_SCALE = 32 ** -0.5
B_SCALE = 64 ** -0.5
CONV = 5
GRID_W = 64
NEG = -1.0e30
MOD_TILES = 72
MOD_PIECES = MOD_TILES // 4

C_NORM, C_BMOD, C_GAIN, C_SUBLN, C_CONVW, C_CONVB = 0, 24, 96, 103, 104, 134
C_DSKIP, C_GNORM, C_SINK, C_DTB, C_ALOG, C_LAM, N_COLS = 140, 144, 148, 152, 153, 154, 282
K_ID, K_MEAN, K_BLK32, K_BLK64, K_C256, K_PERMA, K_PERMB = (P * i for i in range(7))
K_COSA, K_SINA, K_COSB, K_SINB = (7 * P + LAT * i for i in range(4))
K_WIN, K_TRI, K_ONES, K_EPS, K_SIGN, K_BWD, K_FWD, N_CONST = 1920, 2432, 2688, 2816, 2817, 2818, 2819, 2820


def lam_init(layer):
    return 0.8 - 0.6 * math.exp(-0.3 * layer)


def constants():
    k = np.zeros((P, N_CONST), np.float32)
    i = np.arange(P)
    k[:, K_ID:K_ID + P] = np.eye(P)
    k[:, K_MEAN:K_MEAN + P] = 1.0 / D_MODEL
    k[:, K_BLK32:K_BLK32 + P] = (i[:, None] // 32 == i[None, :] // 32) / 32.0
    k[:, K_BLK64:K_BLK64 + P] = (i[:, None] // 64 == i[None, :] // 64) / 64.0
    k[:, K_C256:K_C256 + P] = 1.0 / 256
    t = np.arange(LAT)
    row, col = (t // GRID_W).astype(np.float32), (t % GRID_W).astype(np.float32)
    for dim, perm, cos, sin in ((32, K_PERMA, K_COSA, K_SINA), (64, K_PERMB, K_COSB, K_SINB)):
        q = dim // 4
        for m in range(P):
            if m % (2 * q) < q:
                k[m + q, perm + m] = -1.0
            else:
                k[m - q, perm + m] = 1.0
        inv = (np.float32(10000.0) ** (-np.arange(q, dtype=np.float32) / np.float32(q))).astype(np.float32)
        ar, ac = row[:, None] * inv, col[:, None] * inv
        ang = np.concatenate([ar, ar, ac, ac], axis=-1).T.astype(np.float32)
        k[:, cos:cos + LAT] = np.cos(ang)[i % dim]
        k[:, sin:sin + LAT] = np.sin(ang)[i % dim]
    for qt in range(2):
        far = np.abs(t[None, :] - (qt * P + i)[:, None]) > 128
        k[:, K_WIN + qt * LAT:K_WIN + (qt + 1) * LAT] = np.where(far, NEG, 0.0)
    k[:, K_TRI:K_TRI + P] = np.where(i[None, :] >= i[:, None], 0.0, NEG)
    k[:, K_TRI + P:K_TRI + 2 * P] = np.where(i[None, :] <= i[:, None], 0.0, NEG)
    k[:, K_ONES:K_ONES + P] = 1.0
    k[:, K_EPS] = EPS
    k[:, K_SIGN] = np.where(i < 8, 1.0, -1.0)
    k[:, K_BWD] = np.where(i < 8, 0.0, 1.0)
    k[:, K_FWD] = np.where(i < 8, 1.0, 0.0)
    return k


def backbone(nc, x_in, c_in, const_in, cols_in, mod_in, ffn_in, proj_in, dt_in, out_w_in, out):
    with ExitStack() as ctx:
        def sem(name):
            return ctx.enter_context(nc.semaphore(name))

        def sb(scope, name, shape, dt=F32):
            return scope.enter_context(nc.sbuf_tensor(name, [P] + shape, dt))

        spill = nc.dram_tensor("x_spill", [P, KT * T], F32, kind="Internal").ap()
        rows_dram = nc.dram_tensor("decay_rows", [DEPTH, 16, 2, T], F32, kind="Internal").ap()
        tot_dram = nc.dram_tensor("decay_totals", [DEPTH, 16, TT], F32, kind="Internal").ap()

        ps = ctx.enter_context(nc.psum_tensor("ps", [P, 8, 512], F32))

        const = sb(ctx, "const", [N_CONST])
        cols = sb(ctx, "cols", [DEPTH, N_COLS])
        mod_t = sb(ctx, "mod_t", [2, DEPTH * MOD_TILES])
        mod_acc = sb(ctx, "mod_acc", [2, 4])
        abg = sb(ctx, "abg", [3 * DEPTH, 3, 2, KT])
        small = sb(ctx, "small", [2, 16])
        lam = sb(ctx, "lam", [80])
        h_hi = sb(ctx, "h_hi", [KT, T], F32R)
        h_lo = sb(ctx, "h_lo", [KT, T], F32R)
        raw = sb(ctx, "raw", [3, UNIT])
        w_hi = sb(ctx, "w_hi", [3, UNIT], F32R)
        w_lo = sb(ctx, "w_lo", [3, UNIT], F32R)

        with ExitStack() as ffn:
            x_res = sb(ffn, "x_res", [KT, T])
            cb = sb(ffn, "cb", [2, D_MODEL])
            a_hi = sb(ffn, "a_hi", [2, T], F32R)
            a_lo = sb(ffn, "a_lo", [2, T], F32R)
            sg = sb(ffn, "sg", [2, T])
            gu = sb(ffn, "gu", [2, T])
            mod_raw = sb(ffn, "mod_raw", [2, 2, D_MODEL])
            mod_prod = sb(ffn, "mod_prod", [2, D_MODEL])
            n_acc = sb(ffn, "n_acc", [T])
            n_rstd = sb(ffn, "n_rstd", [T])
            n_t = sb(ffn, "n_t", [2, T])

        mix = ctx.enter_context(ExitStack())
        cv = sb(mix, "cv", [6, T])
        zs = sb(mix, "zs", [4, T])
        xtok = sb(mix, "xtok", [TT, 512])
        btok = sb(mix, "btok", [TT, P])
        cbt = sb(mix, "cbt", [2, TT, P])
        qk = sb(mix, "qk", [7, T])
        with ExitStack() as s:
            rows = sb(s, "rows", [5, T])
            rt = sb(s, "rt", [T])
        vtok = sb(mix, "vtok", [TT, 384])
        st = sb(mix, "st", [2, 3, 256])
        dcol = sb(mix, "dcol", [TT, 80])
        etb = sb(mix, "etb", [2, 4, TT])
        with ExitStack() as s:
            xpad = sb(s, "xpad", [2, 2, 260])
            p_raw = sb(s, "p_raw", [2, T])
            p_sq = sb(s, "p_sq", [2, T])
            p_rst = sb(s, "p_rst", [2, T])
            rtmp = sb(s, "rtmp", [LAT])
        with ExitStack() as s:
            xdec = sb(s, "xdec", [2, 512])
            eo = sb(s, "eo", [2, 2, T])
            dd = sb(s, "dd", [2, T])
            mt = sb(s, "mt", [2, T])
            cexp = sb(s, "cexp", [2, T])
            y_r = sb(s, "y_r", [T])
        with ExitStack() as s:
            e_att = sb(s, "e_att", [2, 2, T])
            a_t = sb(s, "a_t", [2, TT, P])
            f_sq = sb(s, "f_sq", [2, T])
            f_r = sb(s, "f_r", [2, T])

        const_in_s, cols_in_s, x_in_s, cb_in_s = sem("const_in_s"), sem("cols_in_s"), sem("x_in_s"), sem("cb_in_s")
        raw_in = [sem(f"raw_in{i}") for i in range(3)]
        hi_ready, lo_ready, unit_done = sem("hi_ready"), sem("lo_ready"), sem("unit_done")
        mod_in_s = [sem(f"mod_in{i}") for i in range(2)]
        mod_step, mod_put, derive_s = sem("mod_step"), sem("mod_put"), sem("derive_s")
        cb_ready = sem("cb_ready")
        down_done = sem("down_done")
        silu_done, mul_done, act_hi_s, act_lo_s, y_evac = (sem(n) for n in ("silu_done", "mul_done", "act_hi_s", "act_lo_s", "y_evac"))
        sq_done, acc_done, mean_done, rstd_done, t_done, aff_done, h_hi_s, h_lo_s = (
            sem(n) for n in ("sq_done", "acc_done", "mean_done", "rstd_done", "t_done", "aff_done", "h_hi_s", "h_lo_s"))
        spilled, x_back, wo_evac, out_s = sem("spilled"), sem("x_back"), sem("wo_evac"), sem("out_s")
        pj_evac, pads, conv_step, cv_ready = sem("pj_evac"), sem("pads"), sem("conv_step"), sem("cv_ready")
        xt_mm, xt_evac = sem("xt_mm"), sem("xt_evac")
        row_act, row_dve, rows_out, etb_in = sem("row_act"), sem("row_dve"), sem("rows_out"), sem("etb_in")
        qmean, qrst, qk1, rv_mm, rv_evac, qcos, qk_done = (
            sem(n) for n in ("qmean", "qrst", "qk1", "rv_mm", "rv_evac", "qcos", "qk_done"))
        raw_copied = sem("raw_copied")
        xd_done, st_mm, st_step, st_done = sem("xd_done"), sem("st_mm"), sem("st_step"), sem("st_done")
        eo_in = [sem("eo_in0"), sem("eo_in1")]
        d_done, ex_done, cexp_done, mt_done, hd_mm, y_step, y_done = (
            sem(n) for n in ("d_done", "ex_done", "cexp_done", "mt_done", "hd_mm", "y_step", "y_done"))
        sc_mm, mx_done, nmx_done, exp_done, rc_step, a_done, tr_mm, at_evac, pv_mm, ot_evac = (
            sem(n) for n in ("sc_mm", "mx_done", "nmx_done", "exp_done", "rc_step", "a_done", "tr_mm", "at_evac", "pv_mm", "ot_evac"))
        fsq_done, fmean, frst, f_norm, mix_hi_s, mix_lo_s = (
            sem(n) for n in ("fsq_done", "fmean", "frst", "f_norm", "mix_hi_s", "mix_lo_s"))
        lam_s, lam_e = sem("lam_s"), sem("lam_e")

        def ffn_base(f):
            return (f // 2) * LAYER_UNITS + (f % 2) * (FFN_UNITS + MIX_UNITS)

        def mix_base(layer):
            return layer * LAYER_UNITS + FFN_UNITS

        LAST_UNIT = DEPTH * LAYER_UNITS

        def ffn_tokens(f):
            return LAT if f == 3 else T

        def out_tokens(layer):
            return LAT if layer == DEPTH - 1 else T

        def streams(nt):
            return range(nt // LAT)

        def c_(off, n=1):
            return const[:, off:off + n]

        def col(layer, off, n=1, p0=0, p1=P):
            return cols[p0:p1, layer, off:off + n]

        def updated(f, i, d):
            return (f * PAIRS + i) * KT + d + 1 + KT

        MOD_START = (0, 4)
        MOD_PRE = {0: (4, 2), 1: (16, 2)}
        MOD_LOOP = {0: (6, 10), 1: (18, 10), 2: (28, 8)}
        STRETCH = {0: [(1, PAIRS, 6)], 1: [(1, PAIRS, 18)], 2: [(1, 9, 28), (9, PAIRS, None)], 3: [(1, PAIRS - 1, None)]}

        def evacs(m):
            return 2 * (m + 1) if m < DT_UNIT else 2 * m + 1

        RAW_OF = [("n", 0), ("n", 1), ("n", 2), ("n", 3), ("v", 0), ("v", 1), ("n", 4), ("n", 5), ("n", 6), ("v", 2)]
        RV_OF = {("n", 0): 0, ("n", 1): 1, ("n", 2): 2, ("n", 3): 3, ("v", 0): 4, ("v", 1): 5, ("n", 4): 6, ("n", 5): 7, ("n", 6): 8, ("v", 2): 9}
        STEPS = [("U", 0), ("cv", 0), ("cv", 1), ("U", 1), ("cv", 2), ("cv", 3), ("U", 2), ("cv", 4), ("cv", 5),
                 ("U", 3), ("z", 0), ("z", 1), ("U", 4), ("z", 2), ("z", 3), ("U", 5), ("dt", 0),
                 ("U", 6), ("a", 0), ("a", 1)] + [("t", j) for j in range(8)] + [
                 ("U", 7), ("b", 0), ("b", 1), ("a", 2), ("a", 3), ("U", 8), ("c", 0), ("c", 1), ("b", 2), ("b", 3),
                 ("a", 4), ("a", 5), ("U", 9), ("c", 2), ("c", 3), ("v", 0), ("v", 1), ("a", 6), ("a", 7),
                 ("U", 10), ("b", 4), ("b", 5), ("a", 8), ("c", 4), ("c", 5), ("b", 6), ("a", 9), ("v", 2), ("c", 6)]

        ORDER = [[2, 3, 0, 1], [3, 2, 1, 0]]
        PLACE = [[ORDER[d].index(c) for c in range(TT)] for d in range(2)]
        HEADS = 16

        def att_items(layer):
            return [(kind, h, qt) for kind in "AB" for h in range(4) for qt in range(out_tokens(layer) // P)]

        def att_base(layer):
            return layer * len(att_items(0))

        def keys_of(qt):
            return (0, T) if qt < 2 else (LAT, CTX)

        NORM_OF_FFN = [0, 2, 3, 5]
        NORM_AFTER = [(1, T), (3, T), (4, T)]
        AFF_BASE = [2 * KT * n for n in range(6)]
        DERIVED_AB = [3, 8, 12, 17, 22, 26]
        ROW_STEPS = 12

        block = ctx.enter_context(nc.Block())

        @block.sync
        def _(sp):
            def load(u_src, slot, turn, n=UNIT):
                if not (isinstance(turn, int) and turn == 0):
                    sp.wait_ge(lo_ready, 3 * turn + slot - 2)
                sp.dma_start(raw[:, slot, 0:n], u_src).then_inc(raw_in[slot], 16)

            def load_ffn(f):
                base = ffn_base(f) // 3
                load(ffn_in[f, 0], 0, base)
                load(ffn_in[f, 1], 1, base)
                with sp.Fori(1, PAIRS) as i:
                    load(ffn_in[f, 3 * i - 1], 2, base + i - 1)
                    load(ffn_in[f, 3 * i], 0, base + i)
                    load(ffn_in[f, 3 * i + 1], 1, base + i)
                load(ffn_in[f, FFN_UNITS - 1], 2, base + PAIRS - 1)

            def load_mix(layer):
                base = mix_base(layer)
                for m in range(MIX_UNITS):
                    u = base + m
                    if m == 3:
                        sp.wait_ge(t_done, 8 * (3 * layer + 2))
                        sp.dma_start(spill, x_res[:, :, :].rearrange("p k t -> p (k t)")).then_inc(spilled, 16)
                    if m < DT_UNIT:
                        load(proj_in[layer, m], u % 3, u // 3)
                    elif m == DT_UNIT:
                        load(dt_in[layer], u % 3, u // 3, P)
                    elif m < PROJ_UNITS:
                        load(proj_in[layer, m - 1], u % 3, u // 3)
                    else:
                        load(out_w_in[layer, m - PROJ_UNITS], u % 3, u // 3)
                sp.wait_ge(mix_lo_s, 8 * (layer + 1))
                sp.wait_ge(spilled, 16 * (layer + 1))
                sp.dma_start(x_res[:, :, :].rearrange("p k t -> p (k t)"), spill).then_inc(x_back, 16)
                if layer < DEPTH - 1:
                    sp.dma_start(cb[:, :, :], c_in.partition_broadcast(P)).then_inc(cb_in_s, 16)

            sp.dma_start(cb[:, :, :], c_in.partition_broadcast(P)).then_inc(cb_in_s, 16)
            sp.dma_start(x_res[:, :, :], x_in).then_inc(x_in_s, 16)
            sp.dma_start(cols[:, :, :], cols_in).then_inc(cols_in_s, 16)
            sp.dma_start(const[:, :], const_in).then_inc(const_in_s, 16)
            for layer in range(DEPTH):
                load_ffn(2 * layer)
                load_mix(layer)
                load_ffn(2 * layer + 1)
            for d in range(KT):
                sp.wait_ge(y_evac, updated(3, PAIRS - 1, d))
                sp.dma_start(out[:, d, :], x_res[:, d, 0:LAT]).then_inc(out_s, 16)
            sp.wait_ge(out_s, 16 * KT)

        @block.gpsimd
        def _(pool):
            def load_piece(q):
                for half in range(2):
                    if not (isinstance(q, int) and q == 0):
                        pool.wait_ge(mod_step, 8 * q + 4 * half - 4)
                    pool.dma_start(mod_raw[:, half], mod_in[2 * q + half]).then_inc(mod_in_s[half], 16)

            def load_stretches(f):
                for lo, hi, q0 in STRETCH[f]:
                    if q0 is not None:
                        with pool.Fori(lo, hi) as i:
                            load_piece(i + (q0 - lo))

            def mixer_rows(layer):
                pool.wait_ge(row_act, 7 * layer + 7)
                pool.wait_ge(row_dve, ROW_STEPS * (layer + 1))
                pool.dma_start(rows_dram[layer, :, 0, :], rt[0:16, :]).then_inc(rows_out, 16)
                pool.dma_start(rows_dram[layer, :, 1, :], rows[0:16, 4, :]).then_inc(rows_out, 16)
                pool.dma_start(tot_dram[layer], lam[0:16, 72:76]).then_inc(rows_out, 16)
                pool.wait_ge(rows_out, 48 * (layer + 1))
                for g in range(2):
                    src = tot_dram[layer].rearrange("(d g h) c -> g d (h c)", d=2, g=2)[g]
                    pool.dma_start(etb[64 * g:64 * g + 64].rearrange("p d h c -> p d (h c)"),
                                   src.partition_broadcast(64)).then_inc(etb_in, 16)
                nt = out_tokens(layer)
                for r in range(HEADS):
                    h, d = r // 2, r % 2
                    if r < 2:
                        pool.wait_ge(qk_done, 7 * (layer + 1))
                        pool.wait_ge(xt_evac, 8 * (layer + 1))
                        pool.wait_ge(rv_mm, 10 * (layer + 1))
                    else:
                        pool.wait_ge(cexp_done, HEADS * layer + r - 1)
                    pool.dma_start(eo[:, r % 2, :, 0:nt],
                                   rows_dram[layer, 8 * d + h, :, 0:nt].partition_broadcast(P)).then_inc(eo_in[r % 2], 16)

            for q in range(*MOD_START):
                load_piece(q)
            for f in range(4):
                if f in MOD_PRE:
                    if f == 1:
                        pool.wait_ge(mix_lo_s, 8)
                    for q in range(MOD_PRE[f][0], sum(MOD_PRE[f])):
                        load_piece(q)
                load_stretches(f)
                if f % 2 == 0:
                    mixer_rows(f // 2)

        @block.scalar
        def _(act):
            def table_ln_exp():
                act.add_instruction(mybir.InstLoadActFuncSet(
                    name=nc.get_next_instruction_name(), act_func_set_id=LN_EXP_SET,
                    engine=mybir.EngineType.Activation, ins=[], outs=[]))

            def split(slot, turn, n=UNIT):
                act.wait_ge(raw_in[slot], 16 * turn + 16)
                if not (isinstance(turn, int) and turn == 0):
                    act.wait_ge(unit_done, 3 * turn + slot - 2)
                act.activation(w_hi[:, slot, 0:n], raw[:, slot, 0:n], ACT.Copy).then_inc(hi_ready, 1)

            def split_after(u):
                v = u + 3
                if v < LAST_UNIT:
                    split(v % 3, v // 3, P if (v - FFN_UNITS) % LAYER_UNITS == DT_UNIT else UNIT)

            def norm_square(n, d, nt, x_ready):
                act.wait_ge(*x_ready)
                if d == 0:
                    if n:
                        act.wait_ge(mean_done, n)
                    dst = n_acc[:, 0:nt]
                else:
                    if d < 3:
                        if n:
                            act.wait_ge(h_lo_s, 8 * n)
                    else:
                        act.wait_ge(acc_done, 7 * n + d - 2)
                    dst = n_t[:, d % 2, 0:nt]
                act.activation(dst, x_res[:, d, 0:nt], ACT.Square).then_inc(sq_done, 1)

            def norm_rest(n, nt):
                table_ln_exp()
                act.wait_ge(mean_done, n + 1)
                act.activation(n_rstd[:, 0:nt], ps[:, 0, 0:nt], ACT.Ln, bias=c_(K_EPS)).then_inc(rstd_done, 1)
                act.wait_ge(rstd_done, 2 * n + 1)
                act.activation(n_rstd[:, 0:nt], n_rstd[:, 0:nt], ACT.Exp, scale=-0.5).then_inc(rstd_done, 1)
                act.wait_ge(derive_s, DERIVED_AB[n])
                for d in range(KT):
                    act.wait_ge(t_done, 8 * n + d + 1)
                    for s in streams(nt):
                        seg = n_t[:, d % 2, s * LAT:(s + 1) * LAT]
                        act.activation(seg, seg, ACT.Identity, scale=abg[:, n, 0, s, d:d + 1],
                                       bias=abg[:, n, 1, s, d:d + 1]).then_inc(aff_done, 1)
                    act.wait_ge(aff_done, AFF_BASE[n] + len(streams(nt)) * (d + 1))
                    act.activation(h_hi[:, d, 0:nt], n_t[:, d % 2, 0:nt], ACT.Copy).then_inc(h_hi_s, 1)

            def silu_gate(f, i, nt):
                for m in range(2):
                    if not (f == 0 and isinstance(i, int) and i == 0):
                        act.wait_ge(mul_done, 2 * (f * PAIRS + i) - 1 + m)
                    act.activation(sg[:, m, 0:nt], ps[:, m, 0:nt], ACT.Silu).then_inc(silu_done, 1)

            def round_product(f, i, nt):
                for m in range(2):
                    act.wait_ge(mul_done, 2 * (f * PAIRS + i) + m + 1)
                    act.activation(a_hi[:, m, 0:nt], gu[:, m, 0:nt], ACT.Copy).then_inc(act_hi_s, 1)

            def ffn_phase(f):
                nt, base = ffn_tokens(f), ffn_base(f)
                b3 = base // 3
                act.wait_ge(unit_done, base + 1)
                silu_gate(f, 0, nt)
                split_after(base)
                act.wait_ge(unit_done, base + 2)
                round_product(f, 0, nt)
                split_after(base + 1)

                def turn(i, last=False):
                    act.wait_ge(unit_done, base + 3 * i)
                    silu_gate(f, i, nt)
                    split(2, b3 + i)
                    act.wait_ge(unit_done, base + 3 * i + 1)
                    if not last:
                        split(0, b3 + i + 1)
                    act.wait_ge(unit_done, base + 3 * i + 2)
                    round_product(f, i, nt)
                    if not last:
                        split(1, b3 + i + 1)

                for lo, hi, _ in STRETCH[f]:
                    with act.Fori(lo, hi) as i:
                        turn(i)
                if f == 3:
                    turn(PAIRS - 1, last=True)
                if f < 3:
                    n, ntn = NORM_AFTER[f]
                    for d in range(KT):
                        norm_square(n, d, ntn, (y_evac, updated(f, PAIRS - 1, d)))
                    act.wait_ge(unit_done, base + FFN_UNITS)
                    split_after(base + FFN_UNITS - 1)
                    norm_rest(n, ntn)

            def mixer(layer):
                base, nt = mix_base(layer), out_tokens(layer)
                act.wait_ge(spilled, 16 * (layer + 1))
                act.wait_ge(h_lo_s, 8 * (3 * layer + 2))
                for kind, j in STEPS:
                    if kind == "U":
                        act.wait_ge(unit_done, base + j + 1)
                        split_after(base + j)
                        bank = 2 * (j % 2)
                    elif kind == "cv":
                        if j >= 2:
                            act.wait_ge(conv_step, CONV * (6 * layer + j - 1))
                        act.activation(xpad[:, j % 2, :, 2:2 + LAT],
                                       ps[:, bank + j % 2, :].rearrange("p (s t) -> p s t", s=2),
                                       ACT.Copy).then_inc(pj_evac, 1)
                        if j >= 1:
                            conv_silu(layer, j - 1)
                    elif kind == "z":
                        if j == 0:
                            conv_silu(layer, 5)
                        act.activation(zs[:, j, 0:nt], ps[:, bank + j % 2, 0:nt], ACT.Silu).then_inc(pj_evac, 1)
                    elif kind == "dt":
                        decay_rows(layer, bank)
                    elif kind == "t":
                        act.wait_ge(xt_mm, 8 * layer + j + 1)
                        src = ps[:, 4 + j % 4, :]
                        if j < 4:
                            act.activation(xtok[:, j, :], src, ACT.Copy).then_inc(xt_evac, 1)
                        elif j == 4:
                            act.activation(btok[:, :, :], src.rearrange("p (c t) -> p c t", c=TT), ACT.Copy).then_inc(xt_evac, 1)
                        elif j < 7:
                            act.activation(cbt[:, j - 5], src.rearrange("p (c t) -> p c t", c=TT), ACT.Copy).then_inc(xt_evac, 1)
                        else:
                            act.activation(dcol[:, :, :], src[:, 0:TT * 80].rearrange("p (c t) -> p c t", c=TT),
                                           ACT.Copy).then_inc(xt_evac, 1)
                    elif kind == "a":
                        what, i = RAW_OF[j]
                        if j >= 2:
                            before, ib = RAW_OF[j - 2]
                            if before == "n":
                                act.wait_ge(qk1, 7 * layer + ib + 1)
                            else:
                                act.wait_ge(rv_mm, 10 * layer + RV_OF[("v", ib)] + 1)
                        src = ps[:, bank + j % 2, :]
                        cp = act.activation(p_raw[:, j % 2, :], src, ACT.Copy)
                        if what == "n":
                            cp.then_inc(raw_copied, 1)
                            if i >= 2:
                                act.wait_ge(qmean, 7 * layer + i - 1)
                            act.activation(p_sq[:, i % 2, :], src, ACT.Square).then_inc(pj_evac, 1)
                        else:
                            cp.then_inc(pj_evac, 1)
                    elif kind == "b":
                        act.wait_ge(qmean, 7 * layer + j + 1)
                        if j >= 2:
                            act.wait_ge(qk1, 7 * layer + j - 1)
                        act.activation(p_rst[:, j % 2, :], ps[:, 4 + j % 2, :], ACT.Ln, bias=c_(K_EPS)).then_inc(qrst, 1)
                        act.wait_ge(qrst, 2 * (7 * layer + j) + 1)
                        act.activation(p_rst[:, j % 2, :], p_rst[:, j % 2, :], ACT.Exp, scale=-0.5).then_inc(qrst, 1)
                act.wait_ge(lam_s, 4 * layer + 2)
                act.activation(lam[:, 66:68], lam[:, 64:66], ACT.Exp).then_inc(lam_e, 1)
                for r in range(HEADS):
                    act.wait_ge(d_done, HEADS * layer + r + 1)
                    act.activation(dd[:, r % 2, 0:nt], dd[:, r % 2, 0:nt], ACT.Exp).then_inc(ex_done, 1)
                act.wait_ge(mt_done, HEADS * (layer + 1))
                for g in range(2):
                    final_norm(layer, g, nt, zs[:, 2 * g:2 * g + 2, 0:nt], dd[:, :, 0:nt], y_r[:, 0:nt], 2, (y_done, 4 * layer + 2 * g + 2))
                    for t in range(2 * g, 2 * g + 2):
                        act.wait_ge(f_norm, 6 * layer + t + 1)
                        act.activation(h_hi[:, 4 + t, 0:nt], zs[:, t, 0:nt], ACT.Copy).then_inc(mix_hi_s, 1)
                attention(layer)
                for t in range(2):
                    final_norm(layer, 2 + t, nt, cv[:, t, 0:nt], f_sq[:, t, 0:nt], f_r[:, t, 0:nt], 2 + t, (ot_evac, 4 * layer + t + 1))
                    act.wait_ge(f_norm, 6 * layer + 4 + t + 1)
                    act.activation(h_hi[:, t, 0:nt], cv[:, t, 0:nt], ACT.Copy).then_inc(mix_hi_s, 1)
                for t in range(2, 4):
                    act.wait_ge(ot_evac, 4 * layer + t + 1)
                    act.activation(h_hi[:, t, 0:nt], cv[:, t, 0:nt], ACT.Copy).then_inc(mix_hi_s, 1)
                n = 3 * layer + 2
                for q in range(OUT_UNITS):
                    act.wait_ge(unit_done, base + PROJ_UNITS + q + 1)
                    split_after(base + PROJ_UNITS + q)
                    for d in range(2 * q, 2 * q + 2):
                        norm_square(n, d, nt, (wo_evac, 8 * layer + d + 1))
                norm_rest(n, nt)
                if layer == 0:
                    act.wait_ge(cb_in_s, 32)
                    for s in range(2):
                        act.activation(cb[:, s, :], cb[:, s, :], ACT.Silu).then_inc(cb_ready, 1)

            def conv_silu(layer, j):
                act.wait_ge(conv_step, CONV * (6 * layer + j + 1))
                act.activation(cv[:, j, :], cv[:, j, :], ACT.Silu, bias=col(layer, C_CONVB + j)).then_inc(cv_ready, 1)

            def final_norm(layer, k, nt, src, sq, rst, bank, ready):
                act.wait_ge(*ready)
                act.activation(sq, src, ACT.Square).then_inc(fsq_done, 1)
                act.wait_ge(fmean, 4 * layer + k + 1)
                if k == 1:
                    act.wait_ge(f_norm, 6 * layer + 2)
                act.activation(rst, ps[:, bank, 0:nt], ACT.Ln, bias=c_(K_EPS)).then_inc(frst, 1)
                act.wait_ge(frst, 2 * (4 * layer + k) + 1)
                act.activation(rst, rst, ACT.Exp, scale=-0.5).then_inc(frst, 1)

            def decay_rows(layer, bank):
                ra, rd = 7 * layer, ROW_STEPS * layer
                table_ln_exp()
                act.activation(rows[0:16, 0, :], ps[0:16, bank, :], ACT.Identity,
                               bias=col(layer, C_DTB, 1, 0, 16)).then_inc(pj_evac, 1)
                act.wait_ge(pj_evac, 21 * layer + evacs(DT_UNIT))
                act.activation(rows[0:16, 1, :], rows[0:16, 0, :], ACT.Abs).then_inc(row_act, 1)
                act.wait_ge(row_act, ra + 1)
                act.activation(rows[0:16, 1, :], rows[0:16, 1, :], ACT.Exp, scale=-1.0).then_inc(row_act, 1)
                act.activation(lam[0:16, 70:71], col(layer, C_ALOG, 1, 0, 16), ACT.Exp).then_inc(row_act, 1)
                act.wait_ge(row_dve, rd + 1)
                act.activation(rows[0:16, 3, :], rows[0:16, 2, :], ACT.Ln).then_inc(row_act, 1)
                act.wait_ge(row_dve, rd + 10)
                act.activation(rows[0:16, 3, :], rows[0:16, 3, :], ACT.Exp).then_inc(row_act, 1)
                act.wait_ge(row_dve, rd + 12)
                act.activation(rows[0:16, 4, :], rows[0:16, 4, :], ACT.Exp).then_inc(row_act, 1)
                act.activation(lam[0:16, 72:76], rows[0:16, 2, :].rearrange("p (c t) -> p c t", c=TT)[:, :, P - 1],
                               ACT.Exp).then_inc(row_act, 1)

            def attention(layer):
                nt, b = out_tokens(layer), att_base(layer)
                items = att_items(layer)

                def exps(e):
                    kind, h, qt = items[e]
                    k0, nk = keys_of(qt)
                    act.wait_ge(nmx_done, b + e + 1)
                    if e >= 2:
                        act.wait_ge(tr_mm, b + e - 1)
                    for c in range(2 if kind == "A" else 1):
                        x = act.activation(e_att[:, e % 2, c, 0:nk], ps[:, 2 * (e % 2) + c, 0:nk], ACT.Exp,
                                           bias=small[:, e % 2, 2 + c:3 + c],
                                           scale=A_SCALE if kind == "A" else B_SCALE,
                                           accum_out=small[:, e % 2, 4 + c:5 + c])
                    if kind == "B":
                        x = act.activation(small[:, e % 2, 5:6], col(layer, C_SINK + h), ACT.Exp,
                                           bias=small[:, e % 2, 2:3])
                    x.then_inc(exp_done, 1)

                def out_of_psum(e):
                    kind, h, qt = items[e]
                    nk = keys_of(qt)[1]
                    act.wait_ge(tr_mm, b + e + 1)
                    if e >= 2:
                        act.wait_ge(pv_mm, b + e - 1)
                    act.activation(a_t[:, e % 2, 0:nk // P, :], ps[:, 4 + e % 2, 0:nk].rearrange("p (c q) -> p c q", q=P),
                                   ACT.Copy).then_inc(at_evac, 1)

                def out_tile(e):
                    kind, h, qt = items[e]
                    if h % 2 == 1 and qt == nt // P - 1:
                        tile = (0 if kind == "A" else 2) + h // 2
                        act.wait_ge(pv_mm, b + e + 1)
                        act.activation(cv[:, tile, 0:nt], ps[:, 6 + tile % 2, 0:nt], ACT.Copy).then_inc(ot_evac, 1)

                for e in range(len(items) + 2):
                    if e < len(items):
                        exps(e)
                    if 1 <= e <= len(items):
                        out_of_psum(e - 1)
                    if e >= 2:
                        out_tile(e - 2)

            act.wait_ge(cb_in_s, 16)
            for s in range(2):
                act.activation(cb[:, s, :], cb[:, s, :], ACT.Silu).then_inc(cb_ready, 1)
            for d in range(KT):
                norm_square(0, d, T, (x_in_s, 16))
            for slot in range(3):
                split(slot, 0)
            act.wait_ge(const_in_s, 16)
            norm_rest(0, T)
            for layer in range(DEPTH):
                ffn_phase(2 * layer)
                mixer(layer)
                ffn_phase(2 * layer + 1)

        @block.vector
        def _(dve):
            stt, tt, ts = dve.scalar_tensor_tensor, dve.tensor_tensor, dve.tensor_scalar

            def split(slot, turn, n=UNIT):
                dve.wait_ge(hi_ready, 3 * turn + slot + 1)
                tt(w_lo[:, slot, 0:n], raw[:, slot, 0:n], w_hi[:, slot, 0:n], ALU.subtract).then_inc(lo_ready, 1)

            def split_after(u):
                v = u + 3
                if v < LAST_UNIT:
                    split(v % 3, v // 3, P if (v - FFN_UNITS) % LAYER_UNITS == DT_UNIT else UNIT)

            def mod_tile(q, j, first=False):
                if j == 0:
                    if not first:
                        dve.wait_ge(mod_put, q)
                if j % 2 == 0:
                    dve.wait_ge(mod_in_s[j // 2], 16 * q + 16)
                for s in range(2):
                    if not (first and j == 0):
                        dve.wait_ge(mod_step, 8 * q + 2 * j + s - 1)
                    dve.tensor_tensor_reduce(mod_prod[:, s], mod_raw[:, j // 2, j % 2], cb[:, s, :], 1.0, 0.0, ALU.mult,
                                             ALU.add, mod_acc[:, s, j:j + 1]).then_inc(mod_step, 1)
                if j == 3:
                    dve.wait_ge(mod_step, 8 * q + 8)
                    dve.tensor_copy(mod_t[:, :, bass.ds(4 * q, 4)], mod_acc[:, :, :]).then_inc(mod_put, 1)

            def mod_pieces(q0, n):
                for q in range(q0, q0 + n):
                    for j in range(4):
                        mod_tile(q, j, first=(q == 0))

            derived = [0]

            def chained(ins):
                derived[0] += 1
                ins.then_inc(derive_s, 1)
                dve.wait_ge(derive_s, derived[0])

            def derive(n, what):
                layer, k = n // 3, n % 3
                dve.wait_ge(mod_put, MOD_PIECES * layer + 6 * k + (4 if what == "ab" else 6))

                def chunk(i):
                    t0 = layer * MOD_TILES + (3 * k + i) * KT
                    b = cols[:, layer, C_BMOD + (3 * k + i) * KT:C_BMOD + (3 * k + i + 1) * KT]
                    return mod_t[:, :, t0:t0 + KT], b.unsqueeze(1).to_broadcast([P, 2, KT])

                if what == "ab":
                    m, b = chunk(0)
                    chained(tt(abg[:, n, 1], m, b, ALU.add))
                    m, b = chunk(1)
                    chained(tt(abg[:, n, 0], m, b, ALU.add))
                    w = cols[:, layer, C_NORM + k * KT:C_NORM + (k + 1) * KT].unsqueeze(1).to_broadcast([P, 2, KT])
                    chained(stt(out=abg[:, n, 0], in0=abg[:, n, 0], scalar=1.0, in1=w, op0=ALU.add, op1=ALU.mult))
                else:
                    m, b = chunk(2)
                    chained(tt(abg[:, n, 2], m, b, ALU.add))
                    if k != 1:
                        chained(ts(abg[:, n, 2], abg[:, n, 2], 0.5, None, ALU.mult))

            def add_square(n, d, nt):
                dve.wait_ge(sq_done, 8 * n + d + 1)
                if d >= 2:
                    dve.wait_ge(acc_done, 7 * n + d - 1)
                tt(n_acc[:, 0:nt], n_acc[:, 0:nt], n_t[:, d % 2, 0:nt], ALU.add).then_inc(acc_done, 1)

            def norm_rest(n, nt):
                def remainder(d):
                    dve.wait_ge(h_hi_s, 8 * n + d + 1)
                    tt(h_lo[:, d, 0:nt], n_t[:, d % 2, 0:nt], h_hi[:, d, 0:nt], ALU.subtract).then_inc(h_lo_s, 1)

                dve.wait_ge(acc_done, 7 * n + 7)
                dve.wait_ge(rstd_done, 2 * n + 2)
                for d in range(KT):
                    if d >= 2:
                        dve.wait_ge(h_lo_s, 8 * n + d - 1)
                    tt(n_t[:, d % 2, 0:nt], x_res[:, d, 0:nt], n_rstd[:, 0:nt], ALU.mult).then_inc(t_done, 1)
                    if d >= 1:
                        remainder(d - 1)
                remainder(KT - 1)

            def product(f, i, nt):
                for m in range(2):
                    dve.wait_ge(silu_done, 2 * (f * PAIRS + i) + m + 1)
                    if not (f == 0 and isinstance(i, int) and i == 0):
                        dve.wait_ge(act_lo_s, 2 * (f * PAIRS + i) - 1 + m)
                    tt(gu[:, m, 0:nt], ps[:, 2 + m, 0:nt], sg[:, m, 0:nt], ALU.mult).then_inc(mul_done, 1)
                for m in range(2):
                    dve.wait_ge(act_hi_s, 2 * (f * PAIRS + i) + m + 1)
                    tt(a_lo[:, m, 0:nt], gu[:, m, 0:nt], a_hi[:, m, 0:nt], ALU.subtract).then_inc(act_lo_s, 1)

            def update(n, d, bank, nt, done):
                for s in streams(nt):
                    seg = x_res[:, d, s * LAT:(s + 1) * LAT]
                    last = stt(out=seg, in0=ps[:, bank, s * LAT:(s + 1) * LAT], scalar=abg[:, n, 2, s, d:d + 1],
                               in1=seg, op0=ALU.mult, op1=ALU.add)
                last.then_inc(done, 1)

            def ffn_phase(f):
                nt, base = ffn_tokens(f), ffn_base(f)
                b3, n = base // 3, NORM_OF_FFN[f]
                if f in MOD_PRE:
                    if f == 1:
                        dve.wait_ge(cb_ready, 4)
                q0, cnt = MOD_PRE.get(f, (0, 0))
                split_after(base)
                if cnt:
                    mod_pieces(q0, cnt // 2)
                dve.wait_ge(unit_done, base + 2)
                product(f, 0, nt)
                split_after(base + 1)
                if cnt:
                    mod_pieces(q0 + cnt // 2, cnt - cnt // 2)
                derive(n, "g")

                def down(i, units, add_n=None, piece=None):
                    for d in range(KT):
                        if d < KT - 1:
                            dve.wait_ge(down_done, (f * PAIRS + i) * (KT - 1) + d + 1)
                        else:
                            dve.wait_ge(unit_done, units)
                        dve.wait_ge(y_evac, updated(f, i, d) - KT)
                        update(n, d, 4 + d % 4, nt, y_evac)
                        if piece is not None and d in (3, 7):
                            mod_tile(piece, d // 4)
                        if add_n is not None and d >= 2:
                            add_square(add_n[0], d - 1, add_n[1])

                def turn(i, piece, last=False):
                    split(2, b3 + i)
                    down(i - 1, base + 3 * i + 1, piece=piece)
                    if not last:
                        split(0, b3 + i + 1)
                    if piece is not None:
                        mod_tile(piece, 2)
                    dve.wait_ge(unit_done, base + 3 * i + 2)
                    product(f, i, nt)
                    if not last:
                        split(1, b3 + i + 1)
                    if piece is not None:
                        mod_tile(piece, 3)

                for lo, hi, q in STRETCH[f]:
                    with dve.Fori(lo, hi) as i:
                        turn(i, None if q is None else i + (q - lo))
                if f == 3:
                    turn(PAIRS - 1, None, last=True)
                if f < 3:
                    nn, ntn = NORM_AFTER[f]
                    derive(nn, "ab")
                    if nn % 3 == 1:
                        derive(nn, "g")
                        derive(nn + 1, "ab")
                    down(PAIRS - 1, base + FFN_UNITS, add_n=(nn, ntn))
                    add_square(nn, KT - 1, ntn)
                    split_after(base + FFN_UNITS - 1)
                    norm_rest(nn, ntn)
                else:
                    down(PAIRS - 1, base + FFN_UNITS)

            def mixer(layer):
                base, nt = mix_base(layer), out_tokens(layer)
                dve.wait_ge(spilled, 16 * (layer + 1))
                dve.memset(xpad[:, :, :, 0:2], 0.0)
                dve.memset(rt[:, :], 0.0)
                dve.memset(xpad[:, :, :, 2 + LAT:260], 0.0).then_inc(pads, 1)
                lv = cols[:, layer, C_LAM:C_LAM + 128]
                tt(lam[:, 0:64], lv[:, 0:64], lv[:, 64:128], ALU.mult).then_inc(lam_s, 1)
                dve.wait_ge(lam_s, 4 * layer + 1)
                dve.tensor_reduce(lam[:, 64:66], lam[:, 0:64].rearrange("p (a b) -> p a b", a=2), AX_X, ALU.add).then_inc(lam_s, 1)
                ts(lam[:, 69:70], col(layer, C_SUBLN), 1.0 - lam_init(layer), None, ALU.mult).then_inc(lam_s, 1)
                for kind, j in STEPS:
                    if kind == "U":
                        split_after(base + j)
                    elif kind == "cv":
                        conv(layer, j)
                    elif kind == "dt":
                        decay_rows(layer)
                    elif kind == "b":
                        dve.wait_ge(qrst, 2 * (7 * layer + j) + 2)
                        r = RAW_OF.index(("n", j))
                        stt(out=qk[:, j, :], in0=p_raw[:, r % 2, :], scalar=col(layer, C_GAIN + j), in1=p_rst[:, j % 2, :],
                            op0=ALU.mult, op1=ALU.mult).then_inc(qk1, 1)
                    elif kind == "c":
                        rotate(layer, j)
                    elif kind == "v":
                        s = RV_OF[("v", j)]
                        dve.wait_ge(rv_mm, 10 * layer + s + 1)
                        dve.wait_ge(rows_out, 48 * (layer + 1))
                        dve.tensor_copy(vtok[:, :, j * P:(j + 1) * P],
                                        ps[:, 6 + s % 2, :].rearrange("p (c v) -> p c v", c=TT)).then_inc(rv_evac, 1)
                dve.wait_ge(lam_e, layer + 1)
                stt(out=lam[:, 68:69], in0=lam[:, 67:68], scalar=-lam_init(layer), in1=lam[:, 66:67],
                    op0=ALU.add, op1=ALU.subtract).then_inc(lam_s, 1)
                states(layer)
                heads(layer)
                for g in range(2):
                    dve.wait_ge(frst, 2 * (4 * layer + g) + 2)
                    for t in range(2 * g, 2 * g + 2):
                        stt(out=zs[:, t, 0:nt], in0=zs[:, t, 0:nt], scalar=col(layer, C_GNORM + t), in1=y_r[:, 0:nt],
                            op0=ALU.mult, op1=ALU.mult).then_inc(f_norm, 1)
                    for t in range(2 * g, 2 * g + 2):
                        dve.wait_ge(mix_hi_s, 8 * layer + t + 1)
                        tt(h_lo[:, 4 + t, 0:nt], zs[:, t, 0:nt], h_hi[:, 4 + t, 0:nt], ALU.subtract).then_inc(mix_lo_s, 1)
                attention(layer)
                for t in range(2):
                    dve.wait_ge(frst, 2 * (4 * layer + 2 + t) + 2)
                    stt(out=cv[:, t, 0:nt], in0=cv[:, t, 0:nt], scalar=lam[:, 69:70], in1=f_r[:, t, 0:nt],
                        op0=ALU.mult, op1=ALU.mult).then_inc(f_norm, 1)
                for t in range(4):
                    dve.wait_ge(mix_hi_s, 8 * layer + 4 + t + 1)
                    tt(h_lo[:, t, 0:nt], cv[:, t, 0:nt], h_hi[:, t, 0:nt], ALU.subtract).then_inc(mix_lo_s, 1)
                dve.wait_ge(x_back, 16 * (layer + 1))
                n = 3 * layer + 1
                for q in range(OUT_UNITS):
                    dve.wait_ge(unit_done, base + PROJ_UNITS + q + 1)
                    for d in range(2 * q, 2 * q + 2):
                        update(n, d, d % 4, nt, wo_evac)
                    split_after(base + PROJ_UNITS + q)
                    for d in range(max(1, 2 * q - 1), 2 * q + 1):
                        add_square(n + 1, d, nt)
                add_square(n + 1, KT - 1, nt)
                norm_rest(n + 1, nt)

            def conv(layer, j):
                dve.wait_ge(pj_evac, 21 * layer + j + 1)
                o = cv[:, j, :].rearrange("p (s t) -> p s t", s=2)
                step = CONV * (6 * layer + j)
                if j == 0:
                    dve.wait_ge(pads, layer + 1)
                for k in range(CONV):
                    src, w = xpad[:, j % 2, :, k:k + LAT], col(layer, C_CONVW + CONV * j + k)
                    if k == 0:
                        ts(o, src, w, None, ALU.mult).then_inc(conv_step, 1)
                    else:
                        dve.wait_ge(conv_step, step + k)
                        stt(out=o, in0=src, scalar=w, in1=o, op0=ALU.mult, op1=ALU.add).then_inc(conv_step, 1)

            def rotate(layer, j):
                cos, sin = (K_COSA, K_SINA) if j < 4 else (K_COSB, K_SINB)
                s = RV_OF[("n", j)]
                x = qk[:, j, 0:LAT]
                dve.wait_ge(rv_mm, 10 * layer + s + 1)
                if layer or j:
                    dve.wait_ge(qk_done, 7 * layer + j)
                tt(rtmp[:, :], ps[:, 6 + s % 2, 0:LAT], c_(sin, LAT), ALU.mult).then_inc(rv_evac, 1)
                tt(x, x, c_(cos, LAT), ALU.mult).then_inc(qcos, 1)
                dve.wait_ge(rv_evac, 10 * layer + s + 1)
                dve.wait_ge(qcos, 7 * layer + j + 1)
                tt(x, x, rtmp[:, :], ALU.add).then_inc(qk_done, 1)

            def decay_rows(layer):
                n = [ROW_STEPS * layer]

                def step(ins):
                    n[0] += 1
                    ins.then_inc(row_dve, 1)
                    dve.wait_ge(row_dve, n[0])

                xr, e, u, l3, l4 = (rows[0:16, i, :] for i in range(5))
                tiles = "p (c t) -> p c t"
                ra = 7 * layer
                dve.wait_ge(row_act, ra + 2)
                step(ts(u, e, 1.0, None, ALU.add))
                dve.wait_ge(row_act, ra + 4)
                step(stt(out=e, in0=u, scalar=-1.0, in1=e, op0=ALU.add, op1=ALU.subtract))
                step(tt(l3, l3, e, ALU.subtract))
                step(stt(out=rt[32:48, :], in0=xr, scalar=0.0, in1=l3, op0=ALU.max, op1=ALU.add))
                step(stt(out=l4, in0=xr, scalar=0.0, in1=l3, op0=ALU.max, op1=ALU.add))
                step(ts(xr, l4, lam[0:16, 70:71], -1.0, ALU.mult, ALU.mult))
                for c in range(TT):
                    last = dve.tensor_tensor_scan(u[:, c * P:(c + 1) * P], const[0:16, K_ONES:K_ONES + P],
                                                  xr[:, c * P:(c + 1) * P], 0.0, ALU.mult, ALU.add)
                step(last)
                step(ts(xr, xr, const[0:16, K_BWD:K_BWD + 1], None, ALU.mult))
                step(stt(out=rt[0:16, :], in0=u, scalar=const[0:16, K_SIGN:K_SIGN + 1], in1=xr,
                         op0=ALU.mult, op1=ALU.add))
                tot = u.rearrange(tiles, c=TT)[:, :, P - 1:P].to_broadcast([16, TT, P])
                E3 = rt[0:16, :].rearrange(tiles, c=TT)
                step(stt(out=l3.rearrange(tiles, c=TT), in0=tot, scalar=const[0:16, K_FWD:K_FWD + 1], in1=E3,
                         op0=ALU.mult, op1=ALU.subtract))
                dve.wait_ge(row_act, ra + 5)
                step(tt(rt[64:80, :], l4, l3, ALU.mult))
                step(stt(out=l4.rearrange(tiles, c=TT), in0=tot, scalar=const[0:16, K_BWD:K_BWD + 1], in1=E3,
                         op0=ALU.mult, op1=ALU.add))

            def states(layer):
                dve.wait_ge(etb_in, 32 * (layer + 1))
                dve.wait_ge(xt_evac, 8 * (layer + 1))
                dve.wait_ge(qk_done, 7 * (layer + 1))
                dve.wait_ge(qmean, 7 * (layer + 1))
                dve.wait_ge(rv_mm, 10 * (layer + 1))
                dve.wait_ge(rows_out, 48 * (layer + 1))

                def weighted(i):
                    k, d = i // 2, i % 2
                    c = ORDER[d][k]
                    if i >= 2:
                        dve.wait_ge(st_mm, 6 * layer + i - 1)
                    tt(xdec[:, i % 2, :].rearrange("p (h v) -> p h v", h=8), xtok[:, c, :].rearrange("p (h v) -> p h v", h=8),
                       dcol[:, c, 64 + 8 * d:72 + 8 * d].unsqueeze(2).to_broadcast([P, 8, 64]), ALU.mult).then_inc(xd_done, 1)

                weighted(0)
                weighted(1)
                for i in range(6):
                    k, d = i // 2, i % 2
                    c = ORDER[d][k]
                    src = ps[:, 2 + i % 2, 0:256]
                    if k > 0:
                        dve.wait_ge(st_done, 6 * layer + i - 1)
                        tt(st[:, d, k, :].rearrange("p (h v) -> p h v", h=4), st[:, d, k - 1, :].rearrange("p (h v) -> p h v", h=4),
                           etb[:, d, :, c].unsqueeze(2).to_broadcast([P, 4, 64]), ALU.mult).then_inc(st_step, 1)
                        dve.wait_ge(st_step, 4 * layer + i - 1)
                    dve.wait_ge(st_mm, 6 * layer + i + 1)
                    if k == 0:
                        dve.tensor_copy(st[:, d, 0, :], src).then_inc(st_done, 1)
                    else:
                        tt(st[:, d, k, :], st[:, d, k, :], src, ALU.add).then_inc(st_done, 1)
                    if i + 2 < 6:
                        weighted(i + 2)

            def heads(layer):
                nt = out_tokens(layer)
                b = HEADS * layer

                def exponents(r):
                    h, d = r // 2, r % 2
                    g = h // 4
                    dve.wait_ge(eo_in[r % 2], 16 * (8 * layer + r // 2 + 1))
                    if r >= 2:
                        dve.wait_ge(mt_done, b + r - 1)
                    for c in range(nt // P):
                        x = stt(out=dd[:, r % 2, c * P:(c + 1) * P], in0=eo[:, r % 2, 0, c * P:(c + 1) * P],
                                scalar=dcol[:, c, 8 * d + h:8 * d + h + 1], in1=c_(K_TRI + P * d, P),
                                op0=ALU.subtract, op1=ALU.min)
                    x.then_inc(d_done, 1)
                    if r >= 2:
                        dve.wait_ge(hd_mm, b + r - 1)
                    gs = slice(64 * g, 64 * g + 64)
                    tt(cexp[gs, r % 2, 0:nt], cv[gs, 5, 0:nt], eo[gs, r % 2, 1, 0:nt], ALU.mult).then_inc(cexp_done, 1)

                def kernel_matrix(r):
                    h, d = r // 2, r % 2
                    dve.wait_ge(ex_done, b + r + 1)
                    if r >= 2:
                        dve.wait_ge(hd_mm, b + r - 1)
                    for c in range(nt // P):
                        x = stt(out=mt[:, r % 2, c * P:(c + 1) * P], in0=dd[:, r % 2, c * P:(c + 1) * P],
                                scalar=dcol[:, c, 32 + 8 * d + h:33 + 8 * d + h], in1=cbt[:, h // 4, c, :],
                                op0=ALU.mult, op1=ALU.mult)
                    x.then_inc(mt_done, 1)

                def gated(t):
                    dve.wait_ge(hd_mm, b + 4 * t + 4)
                    stt(out=cv[:, t, 0:nt], in0=cv[:, t, 0:nt], scalar=col(layer, C_DSKIP + t), in1=ps[:, t % 2, 0:nt],
                        op0=ALU.mult, op1=ALU.add).then_inc(y_step, 1)
                    dve.wait_ge(y_step, 4 * layer + t + 1)
                    tt(zs[:, t, 0:nt], zs[:, t, 0:nt], cv[:, t, 0:nt], ALU.mult).then_inc(y_done, 1)

                for r in range(HEADS + 1):
                    if r < HEADS:
                        exponents(r)
                    if r >= 1:
                        kernel_matrix(r - 1)
                    if r >= 5 and (r - 5) % 4 == 0:
                        gated((r - 5) // 4)
                gated(3)

            def attention(layer):
                b, items = att_base(layer), att_items(layer)

                def maxima(e):
                    kind, h, qt = items[e]
                    nk, nc_ = keys_of(qt)[1], 2 if kind == "A" else 1
                    sm = small[:, e % 2]
                    dve.wait_ge(sc_mm, b + e + 1)
                    if e >= 2:
                        dve.wait_ge(a_done, b + e - 1)
                    dve.tensor_reduce(sm[:, 0:nc_], ps[:, 2 * (e % 2):2 * (e % 2) + nc_, 0:nk], AX_X, ALU.max).then_inc(mx_done, 1)
                    if kind == "A":
                        dve.wait_ge(mx_done, mxb[0] + 1)
                        mxb[0] += 1
                        ts(sm[:, 2:4], sm[:, 0:2], -A_SCALE, None, ALU.mult).then_inc(nmx_done, 1)
                    else:
                        dve.wait_ge(mx_done, mxb[0] + 1)
                        ts(sm[:, 1:2], sm[:, 0:1], B_SCALE, col(layer, C_SINK + h), ALU.mult, ALU.max).then_inc(mx_done, 1)
                        dve.wait_ge(mx_done, mxb[0] + 2)
                        mxb[0] += 2
                        ts(sm[:, 2:3], sm[:, 1:2], -1.0, None, ALU.mult).then_inc(nmx_done, 1)

                def weights(e):
                    kind, h, qt = items[e]
                    nk = keys_of(qt)[1]
                    sm, p0, p1 = small[:, e % 2], e_att[:, e % 2, 0, 0:nk], e_att[:, e % 2, 1, 0:nk]

                    def step(ins):
                        rcb[0] += 1
                        ins.then_inc(rc_step, 1)
                        dve.wait_ge(rc_step, rcb[0])

                    dve.wait_ge(exp_done, b + e + 1)
                    if kind == "A":
                        step(dve.reciprocal(sm[:, 6:8], sm[:, 4:6]))
                        step(ts(sm[:, 8:9], sm[:, 7:8], lam[:, 68:69], None, ALU.mult))
                        step(ts(p0, p0, sm[:, 6:7], None, ALU.mult))
                        stt(out=p0, in0=p1, scalar=sm[:, 8:9], in1=p0, op0=ALU.mult, op1=ALU.add).then_inc(a_done, 1)
                    else:
                        step(tt(sm[:, 6:7], sm[:, 4:5], sm[:, 5:6], ALU.add))
                        step(dve.reciprocal(sm[:, 7:8], sm[:, 6:7]))
                        ts(p0, p0, sm[:, 7:8], None, ALU.mult).then_inc(a_done, 1)

                for e in range(len(items) + 1):
                    if e < len(items):
                        maxima(e)
                    if e >= 1:
                        weights(e - 1)

            mxb, rcb = [0], [0]
            dve.memset(small[:, :, :], 0.0).then_inc(y_evac, KT)
            dve.wait_ge(cb_ready, 2)
            mod_pieces(0, 1)
            for d in range(1, KT):
                add_square(0, d, T)
            mod_pieces(1, MOD_START[1] - 1)
            for slot in range(3):
                split(slot, 0)
            dve.wait_ge(cols_in_s, 16)
            derive(0, "ab")
            dve.wait_ge(const_in_s, 16)
            norm_rest(0, T)
            for layer in range(DEPTH):
                ffn_phase(2 * layer)
                mixer(layer)
                ffn_phase(2 * layer + 1)

        @block.tensor
        def _(pe):
            def mm3(dst, slot, wsl, hk, nt, first, last):
                hi, lo = hk
                pe.matmul(dst, w_hi[:, slot, wsl], hi, start=first, stop=False)
                pe.matmul(dst, w_hi[:, slot, wsl], lo, start=False, stop=False)
                return pe.matmul(dst, w_lo[:, slot, wsl], hi, start=False, stop=last)

            def hk(k, nt):
                return h_hi[:, k, 0:nt], h_lo[:, k, 0:nt]

            def split_ready(slot, turn):
                pe.wait_ge(lo_ready, 3 * turn + slot + 1)

            def two_tiles(slot, turn, bank, nt, n=None, ready=None):
                split_ready(slot, turn)
                for k in range(KT):
                    if n is not None:
                        pe.wait_ge(h_lo_s, 8 * n + k + 1)
                    for m in range(2):
                        last = mm3(ps[:, bank + m, 0:nt], slot, slice(256 * k + P * m, 256 * k + P * m + P), hk(k, nt), nt,
                                   k == 0, k == KT - 1)
                last.then_inc(unit_done, 1)

            def mean(n, nt):
                pe.wait_ge(acc_done, 7 * n + 7)
                if n == 0:
                    pe.wait_ge(const_in_s, 16)
                pe.matmul(ps[:, 0, 0:nt], c_(K_MEAN, P), n_acc[:, 0:nt], start=True, stop=True).then_inc(mean_done, 1)

            def ffn_phase(f):
                nt, base = ffn_tokens(f), ffn_base(f)
                b3, n = base // 3, NORM_OF_FFN[f]
                two_tiles(0, b3, 0, nt, n)
                two_tiles(1, b3, 2, nt)

                def down(slot, turn_, i):
                    split_ready(slot, turn_)
                    for d in range(KT):
                        pe.wait_ge(y_evac, updated(f, i, d) - 4)
                        for m in range(2):
                            if d == 0:
                                pe.wait_ge(act_lo_s, 2 * (f * PAIRS + i) + m + 1)
                            last = mm3(ps[:, 4 + d % 4, 0:nt], slot, slice(1024 * m + P * d, 1024 * m + P * d + P),
                                       (a_hi[:, m, 0:nt], a_lo[:, m, 0:nt]), nt, m == 0, m == 1)
                        last.then_inc(down_done if d < KT - 1 else unit_done, 1)

                def turn(i):
                    pe.wait_ge(silu_done, 2 * (f * PAIRS + i))
                    two_tiles(2, b3 + i - 1, 0, nt)
                    down(0, b3 + i, i - 1)
                    pe.wait_ge(mul_done, 2 * (f * PAIRS + i))
                    two_tiles(1, b3 + i, 2, nt)

                for lo, hi, _ in STRETCH[f]:
                    with pe.Fori(lo, hi) as i:
                        turn(i)
                if f == 3:
                    turn(PAIRS - 1)
                down(2, b3 + PAIRS - 1, PAIRS - 1)
                if f < 3:
                    mean(*NORM_AFTER[f])

            def turn_tile(dst, src):
                return pe.transpose(dst, src, const[0:src.shape[0], K_ID:K_ID + src.shape[0]])

            def mixer(layer):
                base, nt = mix_base(layer), out_tokens(layer)
                for kind, j in STEPS:
                    if kind == "U":
                        u = base + j
                        bank = 2 * (j % 2)
                        if j >= 2:
                            pe.wait_ge(pj_evac, 21 * layer + evacs(j - 2))
                        if j == DT_UNIT:
                            split_ready(u % 3, u // 3)
                            for k in range(KT):
                                last = mm3(ps[0:16, bank, :], u % 3, slice(16 * k, 16 * k + 16), hk(k, T), T, k == 0, k == KT - 1)
                            last.then_inc(unit_done, 1)
                        else:
                            two_tiles(u % 3, u // 3, bank, T, 3 * layer + 1 if j == 0 else None)
                    elif kind == "t":
                        if j == 0:
                            pe.wait_ge(cv_ready, 6 * (layer + 1))
                        if j == 7:
                            pe.wait_ge(row_dve, ROW_STEPS * layer + 11)
                        if j >= 4:
                            pe.wait_ge(xt_evac, 8 * layer + j - 3)
                        for i in range(TT):
                            dst = ps[:, 4 + j % 4, i * P:(i + 1) * P]
                            if j < 4:
                                last = turn_tile(dst, cv[:, i, j * P:(j + 1) * P])
                            elif j == 4:
                                last = turn_tile(dst, cv[:, 4, i * P:(i + 1) * P])
                            elif j < 7:
                                gs = slice(64 * (j - 5), 64 * (j - 5) + 64)
                                last = pe.matmul(dst, cv[gs, 4, i * P:(i + 1) * P], cv[gs, 5, i * P:(i + 1) * P],
                                                 start=True, stop=True)
                            else:
                                last = turn_tile(ps[:, 7, i * 80:(i + 1) * 80], rt[0:80, i * P:(i + 1) * P])
                        last.then_inc(xt_mm, 1)
                    elif kind == "b":
                        if j == 0:
                            pe.wait_ge(xt_evac, 8 * (layer + 1))
                        r = RAW_OF.index(("n", j))
                        pe.wait_ge(pj_evac, 21 * layer + evacs(5) + r + 1)
                        if j >= 2:
                            pe.wait_ge(qrst, 2 * (7 * layer + j - 2) + 1)
                        pe.matmul(ps[:, 4 + j % 2, :], c_(K_BLK32 if j < 4 else K_BLK64, P), p_sq[:, j % 2, :],
                                  start=True, stop=True).then_inc(qmean, 1)
                    elif kind in "cv" and kind != "cv":
                        s = RV_OF[("n" if kind == "c" else "v", j)]
                        if s >= 2:
                            pe.wait_ge(rv_evac, 10 * layer + s - 1)
                        if kind == "c":
                            pe.wait_ge(qk1, 7 * layer + j + 1)
                            pe.matmul(ps[:, 6 + s % 2, 0:LAT], c_(K_PERMA if j < 4 else K_PERMB, P), qk[:, j, 0:LAT],
                                      start=True, stop=True).then_inc(rv_mm, 1)
                        else:
                            r = RAW_OF.index(("v", j))
                            pe.wait_ge(pj_evac, 21 * layer + evacs(5) + r + 1)
                            for i in range(TT):
                                last = turn_tile(ps[:, 6 + s % 2, i * P:(i + 1) * P], p_raw[:, r % 2, i * P:(i + 1) * P])
                            last.then_inc(rv_mm, 1)
                pe.wait_ge(pj_evac, 21 * (layer + 1))
                states(layer)
                heads(layer)
                for g in range(2):
                    pe.wait_ge(fsq_done, 4 * layer + g + 1)
                    if g:
                        pe.wait_ge(frst, 2 * 4 * layer + 1)
                    for t in range(2):
                        last = pe.matmul(ps[:, 2, 0:nt], c_(K_C256, P), dd[:, t, 0:nt], start=(t == 0), stop=(t == 1))
                    last.then_inc(fmean, 1)
                attention(layer)
                for t in range(2):
                    pe.wait_ge(fsq_done, 4 * layer + 3 + t)
                    pe.matmul(ps[:, 2 + t, 0:nt], c_(K_BLK64, P), f_sq[:, t, 0:nt], start=True, stop=True).then_inc(fmean, 1)
                for q in range(OUT_UNITS):
                    u = base + PROJ_UNITS + q
                    split_ready(u % 3, u // 3)
                    if q == 0:
                        pe.wait_ge(frst, 2 * 4 * (layer + 1))
                    if q >= 2:
                        pe.wait_ge(wo_evac, 8 * layer + 2 * (q - 1))
                    bank = 2 * (q % 2)
                    for i, k in enumerate([4, 5, 6, 7, 0, 1, 2, 3]):
                        if q == 0:
                            pe.wait_ge(mix_lo_s, 8 * layer + i + 1)
                        for m in range(2):
                            last = mm3(ps[:, bank + m, 0:nt], u % 3, slice(256 * k + P * m, 256 * k + P * m + P), hk(k, nt), nt,
                                       i == 0, i == KT - 1)
                    last.then_inc(unit_done, 1)
                mean(3 * layer + 2, nt)

            def states(layer):
                for i in range(6):
                    k, d = i // 2, i % 2
                    c = ORDER[d][k]
                    pe.wait_ge(xd_done, 6 * layer + i + 1)
                    if i >= 2:
                        pe.wait_ge(st_done, 6 * layer + i - 1)
                    for g in range(2):
                        last = pe.matmul(ps[64 * g:64 * g + 64, 2 + i % 2, 0:256], btok[:, c, 64 * g:64 * g + 64],
                                         xdec[:, i % 2, 256 * g:256 * g + 256], start=True, stop=True)
                    last.then_inc(st_mm, 1)
                pe.wait_ge(st_done, 6 * (layer + 1))

            def heads(layer):
                nct = out_tokens(layer) // P
                for r in range(HEADS):
                    h, d = r // 2, r % 2
                    g, hh, t = h // 4, h % 4, h // 2
                    if h % 2 == 0 and d == 0 and t >= 2:
                        pe.wait_ge(y_step, 4 * layer + t - 1)
                    pe.wait_ge(mt_done, HEADS * layer + r + 1)
                    pe.wait_ge(cexp_done, HEADS * layer + r + 1)
                    rows_ = slice(64 * (h % 2), 64 * (h % 2) + 64)
                    gs = slice(64 * g, 64 * g + 64)
                    for c in range(nct):
                        dst = ps[rows_, t % 2, c * P:(c + 1) * P]
                        k = PLACE[d][c]
                        last = pe.matmul(dst, xtok[:, c, 64 * h:64 * h + 64], mt[:, r % 2, c * P:(c + 1) * P],
                                         start=(d == 0 and c == 0), stop=(d == 1 and k == 0), skip_group_check=True)
                        if k > 0:
                            last = pe.matmul(dst, st[gs, d, k - 1, 64 * hh:64 * hh + 64], cexp[gs, r % 2, c * P:(c + 1) * P],
                                             start=False, stop=(d == 1), skip_group_check=True)
                    last.then_inc(hd_mm, 1)

            def attention(layer):
                b, items, nt = att_base(layer), att_items(layer), out_tokens(layer)

                def scores(e):
                    kind, h, qt = items[e]
                    k0, nk = keys_of(qt)
                    if e >= 2:
                        pe.wait_ge(exp_done, b + e - 1)
                    bank = 2 * (e % 2)
                    qs = slice(qt * P, qt * P + P)
                    if kind == "A":
                        for c in range(2):
                            p0 = 32 * (2 * (h % 2) + c)
                            last = pe.matmul(ps[:, bank + c, 0:nk], qk[p0:p0 + 32, h // 2, qs], qk[p0:p0 + 32, 2 + h // 2, k0:k0 + nk],
                                             start=True, stop=True)
                    else:
                        p0 = 64 * (h // 2)
                        q = qk[p0:p0 + 64, 4 + h % 2, qs]
                        if qt < 2:
                            pe.matmul(ps[:, bank, 0:LAT], q, qk[p0:p0 + 64, 6, 0:LAT], start=True, stop=False)
                            pe.matmul(ps[:, bank, 0:LAT], c_(K_ID, P), c_(K_WIN + LAT * qt, LAT), start=False, stop=True)
                            last = pe.matmul(ps[:, bank, LAT:T], q, qk[p0:p0 + 64, 6, LAT:T], start=True, stop=True)
                        else:
                            last = pe.matmul(ps[:, bank, 0:nk], q, qk[p0:p0 + 64, 6, k0:k0 + nk], start=True, stop=True)
                    last.then_inc(sc_mm, 1)

                def turned(e):
                    kind, h, qt = items[e]
                    pe.wait_ge(a_done, b + e + 1)
                    if e >= 2:
                        pe.wait_ge(at_evac, b + e - 1)
                    for i in range(keys_of(qt)[1] // P):
                        last = turn_tile(ps[:, 4 + e % 2, i * P:(i + 1) * P], e_att[:, e % 2, 0, i * P:(i + 1) * P])
                    last.then_inc(tr_mm, 1)

                def values(e):
                    kind, h, qt = items[e]
                    k0, nk = keys_of(qt)
                    tile = (0 if kind == "A" else 2) + h // 2
                    pe.wait_ge(at_evac, b + e + 1)
                    if h % 2 == 0 and qt == 0 and tile >= 2:
                        pe.wait_ge(ot_evac, 4 * layer + tile - 1)
                    v0 = 64 * h if kind == "A" else 256 + 64 * (h // 2)
                    p0 = 64 * (h % 2)
                    nk_t = nk // P
                    for i in range(nk_t):
                        last = pe.matmul(ps[p0:p0 + 64, 6 + tile % 2, qt * P:(qt + 1) * P], vtok[:, k0 // P + i, v0:v0 + 64],
                                         a_t[:, e % 2, i, :], start=(i == 0), stop=(i == nk_t - 1))
                    last.then_inc(pv_mm, 1)

                n = len(items)
                pe.wait_ge(qk_done, 7 * (layer + 1))
                pe.wait_ge(rv_evac, 10 * (layer + 1))
                pe.wait_ge(y_step, 4 * (layer + 1))
                pe.wait_ge(frst, 2 * (4 * layer + 1) + 1)
                scores(0)
                for e in range(n + 1):
                    if e + 1 < n:
                        scores(e + 1)
                    if e < n:
                        turned(e)
                    if e >= 1:
                        values(e - 1)

            mean(0, T)
            for layer in range(DEPTH):
                ffn_phase(2 * layer)
                mixer(layer)
                ffn_phase(2 * layer + 1)


def layouts(a):
    f = np.ascontiguousarray

    def tile_cols(v, n):
        return np.moveaxis(v.reshape(v.shape[:-1] + (n, P)), -1, 0)

    def unit(w):
        return w.reshape(KT, P, 256).transpose(1, 0, 2).reshape(P, UNIT)

    x = np.concatenate([a["x"][0], a["ctx"][0]], axis=0).T.reshape(KT, P, T).transpose(1, 0, 2)
    c = np.concatenate([a["c"], a["c_ctx"][None]], axis=0)
    mod = a["w_mod"].transpose(0, 2, 1).reshape(DEPTH * MOD_TILES // 2, 2, P, D_MODEL).transpose(0, 2, 1, 3)
    ffn = []
    for layer in range(DEPTH):
        for w13, w2 in ((a["ffn1_w13"][layer], a["ffn1_w2"][layer]), (a["ffn2_w13"][layer], a["ffn2_w2"][layer])):
            gate = [unit(w13[:, 256 * i:256 * i + 256]) for i in range(PAIRS)]
            up = [unit(w13[:, D_FF + 256 * i:D_FF + 256 * i + 256]) for i in range(PAIRS)]
            down = [w2[256 * i:256 * i + 256].reshape(2, P, D_MODEL).transpose(1, 0, 2).reshape(P, UNIT) for i in range(PAIRS)]
            order = [gate[0], up[0]]
            for i in range(1, PAIRS):
                order += [gate[i], down[i - 1], up[i]]
            ffn.append(np.stack(order + [down[PAIRS - 1]]))
    z0, x0, q0 = 1280, 1280 + 512, 768
    cols = np.concatenate([np.arange(x0, x0 + 768), np.arange(z0, z0 + 512), np.arange(768)]
                          + [np.arange(q0 + 64 * h, q0 + 64 * h + 64) for h in (0, 2, 1, 3)] + [np.arange(q0 + 256, q0 + 512)])
    proj = np.stack([np.stack([unit(a["w_in"][layer][:, cols[256 * i:256 * i + 256]]) for i in range(10)]) for layer in range(DEPTH)])
    dt = np.stack([a["w_in"][layer][:, 2560:2576].reshape(KT, P, 16).transpose(1, 0, 2).reshape(P, P) for layer in range(DEPTH)])
    outw = np.stack([np.stack([unit(a["w_out"][layer][:, 256 * i:256 * i + 256]) for i in range(OUT_UNITS)]) for layer in range(DEPTH)])

    def layer_cols(layer):
        def g(name):
            return a[name][layer]

        def every(v):
            return np.broadcast_to(v[None, :], (P, v.shape[0]))

        def rep(v):
            return np.tile(v, P // v.shape[0])[:, None]

        rows16 = [np.tile(g(name).reshape(16), 8)[:, None] for name in ("dt_bias", "a_log")]
        return np.concatenate(
            [tile_cols(g(n), KT) for n in ("norm_ffn1", "norm_mix", "norm_ffn2")] + [tile_cols(g("b_mod"), MOD_TILES)]
            + [rep(g(n)) for n in ("qn_a", "qn_a", "kn_a", "kn_a", "qn_b", "qn_b", "kn_b", "subln_a")]
            + [g("conv_w").reshape(CONV, 6, P).transpose(2, 1, 0).reshape(P, 6 * CONV), tile_cols(g("conv_b"), 6)]
            + [np.repeat(g("d_skip"), 64).reshape(4, P).T, tile_cols(g("gnorm_c"), 4), every(g("sink_b"))] + rows16
            + [every(g(n)) for n in ("lam_q1", "lam_q2", "lam_k1", "lam_k2")], axis=1)

    params = np.stack([layer_cols(layer) for layer in range(DEPTH)], axis=1)
    assert params.shape == (P, DEPTH, N_COLS)
    return {"x_in": f(x), "c_in": f(c), "const_in": constants(), "cols_in": f(params), "mod_in": f(mod),
            "ffn_in": f(np.stack(ffn)), "proj_in": f(proj), "dt_in": f(dt), "out_w_in": f(outw)}


def kernel(**inputs):
    import concourse.bacc as bacc
    from concourse.bass_utils import run_bass_kernel_spmd

    arrays = layouts({k: np.asarray(v) for k, v in inputs.items()})
    nc = bacc.Bacc("TRN2", target_bir_lowering=False, num_devices=1)
    args = [nc.dram_tensor(n, v.shape, mybir.dt.from_np(v.dtype), kind="ExternalInput").ap() for n, v in arrays.items()]
    out = nc.dram_tensor("out", (P, KT, LAT), F32, kind="ExternalOutput").ap()
    backbone(nc, *args, out)
    r = run_bass_kernel_spmd(nc, [arrays], core_ids=[0])
    y = r.results[0]["out"]
    return np.ascontiguousarray(y.transpose(2, 1, 0).reshape(1, LAT, D_MODEL))
```
